# Optimizing a Trainium2 kernel written in Bass

```python
import math
import jax
import jax.numpy as jnp
from jax import lax
import numpy as np

D_MODEL = 1024
BATCH = 1
SEQ = 128
DEPTH = 2
DEC_BATCH = 1
DEC_SEQ = 512
PAST_LEN = 128

GRID_W = 64
EPS = 1e-6
MIX_WIDTH = D_MODEL
POOL_WIDTH = D_MODEL // 4
POOL_GROUPS = 4
POOL_GROUP_DIM = POOL_WIDTH // POOL_GROUPS
POOL_WINDOWS = (2, 4, 8, 16)
GLA_HEADS = 4
GLA_DV = 64
GLA_DK = 32
GLA_WIDTH = GLA_HEADS * GLA_DV
GLA_GATE_RANK = 16
GLA_GATE_TAU = 16.0
GLA_CHUNK = 64
ATTN_HEADS = 8
ATTN_KV_HEADS = 2
ATTN_GROUP = ATTN_HEADS // ATTN_KV_HEADS
HEAD_DIM = 64
ATTN_WIDTH = ATTN_HEADS * HEAD_DIM
WINDOW = 128
ATTN_BLOCK = 128
ROPE_THETA = 10000.0
NEG_INF = -1e30
PEER_HEADS = 8
PEER_N_KEYS = 128
PEER_N_EXPERTS = PEER_N_KEYS * PEER_N_KEYS
PEER_QUERY_DIM = 128
PEER_TOPK = 16
PEER_TOKEN_BLOCK = 128
IN_SIZES = (POOL_WIDTH, GLA_HEADS * GLA_DK, GLA_HEADS * GLA_DK, GLA_WIDTH, GLA_WIDTH, GLA_GATE_RANK, GLA_GATE_RANK, ATTN_HEADS * HEAD_DIM, ATTN_KV_HEADS * HEAD_DIM, ATTN_KV_HEADS * HEAD_DIM)
IN_WIDTH = 1824

kernel_name = 'hybrid_pool_gla_swa_peer_dit_step'

def _rmsnorm(x, g):
    xf = x.astype(jnp.float32)
    y = xf * lax.rsqrt(jnp.mean(xf * xf, axis=-1, keepdims=True) + EPS)
    return (y * g.astype(jnp.float32)).astype(x.dtype)

def _split_proj(p):
    cuts = np.cumsum(IN_SIZES)[:-1].tolist()
    return jnp.split(p, cuts, axis=-1)

def _pool_mix(x, w, scale):
    B, T, _ = x.shape
    xg = x.reshape(B, T, POOL_GROUPS, POOL_GROUP_DIM)
    cs = jnp.concatenate([jnp.zeros((B, 1, POOL_GROUPS, POOL_GROUP_DIM), jnp.float32),
                          jnp.cumsum(xg.astype(jnp.float32), axis=1)], axis=1)
    t = jnp.arange(T)
    diffs = []
    for g, win in enumerate(POOL_WINDOWS):
        left = win // 2
        right = win - 1 - left
        lo = jnp.maximum(t - left, 0)
        hi = jnp.minimum(t + right + 1, T)
        csg = cs[:, :, g]
        mean = (csg[:, hi] - csg[:, lo]) / (hi - lo).astype(jnp.float32)[None, :, None]
        diffs.append(mean.astype(x.dtype) - xg[:, :, g])
    d = jnp.stack(diffs, axis=2)
    y = jnp.einsum('btgc,gcd->btgd', d, w)
    return y.reshape(B, T, POOL_WIDTH) * scale

def _gla_log_decay(z, w2, b2):
    B, T, _ = z.shape
    logit = (z @ w2 + b2).astype(jnp.float32)
    return (jax.nn.log_sigmoid(logit) / GLA_GATE_TAU).reshape(B, T, GLA_HEADS, GLA_DK)

def _gla_scan(q, k, v, log_a, s0):
    B, T, H, dk = q.shape
    dv = v.shape[-1]
    C = GLA_CHUNK
    nc = T // C

    def chunks(a):
        return a.astype(jnp.float32).reshape(B, nc, C, H, a.shape[-1]).transpose(1, 0, 3, 2, 4)

    qc, kc, vc, ac = chunks(q), chunks(k), chunks(v), chunks(log_a)
    causal = jnp.tril(jnp.ones((C, C), dtype=bool))[:, :, None]

    def step(S, inp):
        qb, kb, vb, ab = inp
        b = jnp.cumsum(ab, axis=2)
        inter = jnp.einsum('bhtd,bhde->bhte', qb * jnp.exp(b), S)
        diff = b[:, :, :, None, :] - b[:, :, None, :, :]
        decay = jnp.where(causal, jnp.exp(jnp.where(causal, diff, 0.0)), 0.0)
        scores = jnp.einsum('bhtd,bhsd,bhtsd->bhts', qb, kb, decay)
        intra = jnp.einsum('bhts,bhse->bhte', scores, vb)
        b_last = b[:, :, -1:, :]
        S_new = jnp.exp(b_last[:, :, 0, :])[..., None] * S + jnp.einsum('bhsd,bhse->bhde', kb * jnp.exp(b_last - b), vb)
        return S_new, inter + intra

    S, o = lax.scan(step, s0.astype(jnp.float32), (qc, kc, vc, ac))
    o = o.transpose(1, 0, 3, 2, 4).reshape(B, T, H, dv)
    return o.astype(v.dtype), S.astype(s0.dtype)

def _gla_bidir(q, k, v, la_f, la_b, s0_f, s0_b):
    o_f, s_f = _gla_scan(q, k, v, la_f, s0_f)
    rev = lambda a: jnp.flip(a, axis=1)
    o_b, s_b = _gla_scan(rev(q), rev(k), rev(v), rev(la_b), s0_b)
    return o_f + rev(o_b), s_f, s_b

def _gla_output(o, g, norm_g):
    B, T, H, dv = o.shape
    of = o.astype(jnp.float32)
    of = of * lax.rsqrt(jnp.mean(of * of, axis=-1, keepdims=True) + EPS)
    of = of * norm_g.reshape(H, dv).astype(jnp.float32)
    return of.reshape(B, T, H * dv).astype(o.dtype) * jax.nn.silu(g)

def _axial_rope(x, pos_row, pos_col):
    half = HEAD_DIM // 2
    nf = half // 2
    freqs = ROPE_THETA ** (-jnp.arange(nf, dtype=jnp.float32) / nf)

    def rot(xa, pos):
        ang = pos.astype(jnp.float32)[:, None] * freqs[None, :]
        cos = jnp.cos(ang)[None, :, None, :]
        sin = jnp.sin(ang)[None, :, None, :]
        x1, x2 = xa[..., :nf], xa[..., nf:]
        return jnp.concatenate([x1 * cos - x2 * sin, x1 * sin + x2 * cos], axis=-1)

    xf = x.astype(jnp.float32)
    return jnp.concatenate([rot(xf[..., :half], pos_row), rot(xf[..., half:], pos_col)], axis=-1).astype(x.dtype)

def _context_attention(q, k, v, sink):
    B, T, _, _ = q.shape
    nqb = T // ATTN_BLOCK
    scale = HEAD_DIM ** -0.5
    qb = q.reshape(B, nqb, ATTN_BLOCK, ATTN_KV_HEADS, ATTN_GROUP, HEAD_DIM).transpose(1, 0, 2, 3, 4, 5)
    sink_b = sink.reshape(ATTN_KV_HEADS, ATTN_GROUP).astype(jnp.float32)

    def one(qblk):
        s = jnp.einsum('bqgrd,bkgd->bgrqk', qblk, k).astype(jnp.float32) * scale
        sk = jnp.broadcast_to(sink_b[None, :, :, None, None], s.shape[:-1] + (1,))
        p = jax.nn.softmax(jnp.concatenate([s, sk], axis=-1), axis=-1)[..., :-1]
        return jnp.einsum('bgrqk,bkgd->bqgrd', p.astype(v.dtype), v)

    o = lax.map(one, qb)
    return o.transpose(1, 0, 2, 3, 4, 5).reshape(B, T, ATTN_WIDTH)

def _latent_attention(q, k, v, ck, cv, sink):
    B, T, _, _ = q.shape
    nb = T // ATTN_BLOCK
    scale = HEAD_DIM ** -0.5
    qb = q.reshape(B, nb, ATTN_BLOCK, ATTN_KV_HEADS, ATTN_GROUP, HEAD_DIM)
    pad = jnp.zeros((B, ATTN_BLOCK, ATTN_KV_HEADS, HEAD_DIM), k.dtype)

    def band(a):
        ap = jnp.concatenate([pad, a, pad], axis=1).reshape(B, nb + 2, ATTN_BLOCK, ATTN_KV_HEADS, HEAD_DIM)
        return jnp.concatenate([ap[:, :-2], ap[:, 1:-1], ap[:, 2:]], axis=2)

    kw, vw = band(k), band(v)
    blk = jnp.arange(nb)
    qpos = blk[:, None] * ATTN_BLOCK + jnp.arange(ATTN_BLOCK)[None, :]
    kpos = (blk[:, None] - 1) * ATTN_BLOCK + jnp.arange(3 * ATTN_BLOCK)[None, :]
    mask = ((jnp.abs(qpos[:, :, None] - kpos[:, None, :]) <= WINDOW)
            & (kpos >= 0)[:, None, :] & (kpos < T)[:, None, :])
    s_loc = jnp.einsum('bnqgrd,bnkgd->bngrqk', qb, kw).astype(jnp.float32) * scale
    s_loc = jnp.where(mask[None, :, None, None], s_loc, NEG_INF)
    s_ctx = jnp.einsum('bnqgrd,bkgd->bngrqk', qb, ck).astype(jnp.float32) * scale
    s_sink = jnp.broadcast_to(sink.reshape(ATTN_KV_HEADS, ATTN_GROUP).astype(jnp.float32)[None, None, :, :, None, None],
                              s_loc.shape[:-1] + (1,))
    p = jax.nn.softmax(jnp.concatenate([s_loc, s_ctx, s_sink], axis=-1), axis=-1)
    L = 3 * ATTN_BLOCK
    Lc = ck.shape[1]
    out = (jnp.einsum('bngrqk,bnkgd->bnqgrd', p[..., :L].astype(v.dtype), vw)
           + jnp.einsum('bngrqk,bkgd->bnqgrd', p[..., L:L + Lc].astype(v.dtype), cv))
    return out.reshape(B, T, ATTN_WIDTH)

def _peer(h, wq, subkeys, u, v):
    B, T, D = h.shape
    n = B * T
    hf = h.reshape(n, D)
    q = (hf @ wq).reshape(n, PEER_HEADS, 2, PEER_QUERY_DIM // 2)
    s = jnp.einsum('nhpd,hpkd->nhpk', q, subkeys).astype(jnp.float32)
    sv, si = lax.top_k(s, PEER_TOPK)
    cand = (sv[:, :, 0, :, None] + sv[:, :, 1, None, :]).reshape(n, PEER_HEADS, PEER_TOPK * PEER_TOPK)
    cand_idx = (si[:, :, 0, :, None] * PEER_N_KEYS + si[:, :, 1, None, :]).reshape(n, PEER_HEADS, PEER_TOPK * PEER_TOPK)
    top_v, top_pos = lax.top_k(cand, PEER_TOPK)
    experts = jnp.take_along_axis(cand_idx, top_pos, axis=-1)
    gates = jax.nn.softmax(top_v, axis=-1).astype(h.dtype)
    nblk = n // PEER_TOKEN_BLOCK
    xs = (hf.reshape(nblk, PEER_TOKEN_BLOCK, D),
          experts.reshape(nblk, PEER_TOKEN_BLOCK, PEER_HEADS * PEER_TOPK),
          gates.reshape(nblk, PEER_TOKEN_BLOCK, PEER_HEADS * PEER_TOPK))

    def blk_fn(args):
        xb, eb, gb = args
        act = jax.nn.gelu(jnp.einsum('td,tkd->tk', xb, u[eb]), approximate=False)
        return jnp.einsum('tk,tkd->td', gb * act, v[eb])

    y = lax.map(blk_fn, xs)
    return y.reshape(B, T, D)

def _trunk_layer(x, cvec, lp, ctx, pos):
    (w_ada, b_ada, n1, n2, w_in, pool_w, pool_scale, gla_w_f, gla_b_f, gla_w_b, gla_b_b,
     gla_norm, sink, w_out, peer_wq, peer_subkeys, peer_u, peer_v) = lp
    B, T, _ = x.shape
    sh1, sc1, gt1, sh2, sc2, gt2 = jnp.split(jax.nn.silu(cvec) @ w_ada + b_ada, 6, axis=-1)
    h = _rmsnorm(x, n1) * (1 + sc1) + sh1
    p_pool, gq, gk, gv, gg, gz_f, gz_b, aq, ak, av = _split_proj(h @ w_in)
    y_pool = _pool_mix(p_pool, pool_w, pool_scale)
    gq = gq.reshape(B, T, GLA_HEADS, GLA_DK) * GLA_DK ** -0.5
    gk = gk.reshape(B, T, GLA_HEADS, GLA_DK)
    gv = gv.reshape(B, T, GLA_HEADS, GLA_DV)
    la_f = _gla_log_decay(gz_f, gla_w_f, gla_b_f)
    la_b = _gla_log_decay(gz_b, gla_w_b, gla_b_b)
    aq = aq.reshape(B, T, ATTN_HEADS, HEAD_DIM)
    ak = ak.reshape(B, T, ATTN_KV_HEADS, HEAD_DIM)
    av = av.reshape(B, T, ATTN_KV_HEADS, HEAD_DIM)
    if ctx is None:
        s0 = jnp.zeros((B, GLA_HEADS, GLA_DK, GLA_DV), x.dtype)
        o, s_f, s_b = _gla_bidir(gq, gk, gv, la_f, la_b, s0, s0)
        y_attn = _context_attention(aq, ak, av, sink)
    else:
        ck, cv, s0_f, s0_b = ctx
        o, s_f, s_b = _gla_bidir(gq, gk, gv, la_f, la_b, s0_f, s0_b)
        pos_row, pos_col = pos
        aq = _axial_rope(aq, pos_row, pos_col)
        ak = _axial_rope(ak, pos_row, pos_col)
        y_attn = _latent_attention(aq, ak, av, ck, cv, sink)
    y_gla = _gla_output(o, gg, gla_norm)
    mix = jnp.concatenate([y_pool, y_gla, y_attn], axis=-1)
    x = x + gt1 * (mix @ w_out)
    h2 = _rmsnorm(x, n2) * (1 + sc2) + sh2
    x = x + gt2 * _peer(h2, peer_wq, peer_subkeys, peer_u, peer_v)
    return x, ak, av, s_f, s_b

def setup_inputs(seed: int = 0) -> dict:
    key = jax.random.key(seed)
    ks = jax.random.split(key, 27)
    D = D_MODEL

    def nrm(k, shape, s):
        return s * jax.random.normal(k, shape, jnp.float32)

    return {
        'x_prompt': nrm(ks[0], (BATCH, SEQ, D), 1.0),
        'x_sample': nrm(ks[1], (DEC_BATCH, DEC_SEQ, D), 1.0),
        'cache_k': nrm(ks[2], (DEC_BATCH, DEPTH, PAST_LEN, ATTN_KV_HEADS, HEAD_DIM), 1.0),
        'cache_v': nrm(ks[3], (DEC_BATCH, DEPTH, PAST_LEN, ATTN_KV_HEADS, HEAD_DIM), 1.0),
        'state_fwd': nrm(ks[4], (DEC_BATCH, DEPTH, GLA_HEADS, GLA_DK, GLA_DV), 0.5),
        'state_bwd': nrm(ks[5], (DEC_BATCH, DEPTH, GLA_HEADS, GLA_DK, GLA_DV), 0.5),
        'c': nrm(ks[6], (DEC_BATCH, D), 1.0),
        'c_ctx': nrm(ks[7], (D,), 1.0),
        'w_ada': nrm(ks[8], (DEPTH, D, 6 * D), 0.5 * D ** -0.5),
        'b_ada': nrm(ks[9], (DEPTH, 6 * D), 0.01),
        'norm1_g': 1.0 + nrm(ks[10], (DEPTH, D), 0.02),
        'norm2_g': 1.0 + nrm(ks[11], (DEPTH, D), 0.02),
        'w_in': nrm(ks[12], (DEPTH, D, IN_WIDTH), D ** -0.5),
        'pool_w': nrm(ks[13], (DEPTH, POOL_GROUPS, POOL_GROUP_DIM, POOL_GROUP_DIM), POOL_GROUP_DIM ** -0.5),
        'pool_scale': 1.0 + nrm(ks[14], (DEPTH, POOL_WIDTH), 0.1),
        'gla_gate_w_f': nrm(ks[15], (DEPTH, GLA_GATE_RANK, GLA_HEADS * GLA_DK), GLA_GATE_RANK ** -0.5),
        'gla_gate_b_f': nrm(ks[16], (DEPTH, GLA_HEADS * GLA_DK), 0.01),
        'gla_gate_w_b': nrm(ks[17], (DEPTH, GLA_GATE_RANK, GLA_HEADS * GLA_DK), GLA_GATE_RANK ** -0.5),
        'gla_gate_b_b': nrm(ks[18], (DEPTH, GLA_HEADS * GLA_DK), 0.01),
        'gla_norm_g': 1.0 + nrm(ks[19], (DEPTH, GLA_WIDTH), 0.02),
        'attn_sink': nrm(ks[20], (DEPTH, ATTN_HEADS), 0.5),
        'w_out': nrm(ks[21], (DEPTH, MIX_WIDTH, D), MIX_WIDTH ** -0.5),
        'peer_wq': nrm(ks[22], (DEPTH, D, PEER_HEADS * PEER_QUERY_DIM), D ** -0.5),
        'peer_subkeys': nrm(ks[23], (DEPTH, PEER_HEADS, 2, PEER_N_KEYS, PEER_QUERY_DIM // 2), (PEER_QUERY_DIM // 2) ** -0.5),
        'peer_u': nrm(ks[24], (DEPTH, PEER_N_EXPERTS, D), D ** -0.5),
        'peer_v': nrm(ks[25], (DEPTH, PEER_N_EXPERTS, D), D ** -0.5),
        'final_norm_g': 1.0 + nrm(ks[26], (D,), 0.02),
    }

def reference(x_prompt, x_sample, cache_k, cache_v, state_fwd, state_bwd, c, c_ctx,
              w_ada, b_ada, norm1_g, norm2_g, w_in, pool_w, pool_scale,
              gla_gate_w_f, gla_gate_b_f, gla_gate_w_b, gla_gate_b_b, gla_norm_g,
              attn_sink, w_out, peer_wq, peer_subkeys, peer_u, peer_v, final_norm_g):
    layer_params = (w_ada, b_ada, norm1_g, norm2_g, w_in, pool_w, pool_scale,
                    gla_gate_w_f, gla_gate_b_f, gla_gate_w_b, gla_gate_b_b, gla_norm_g,
                    attn_sink, w_out, peer_wq, peer_subkeys, peer_u, peer_v)
    xc = x_prompt
    c_ctx_b = c_ctx[None, None, :]
    ks_l, vs_l, sf_l, sb_l = [], [], [], []
    for l in range(DEPTH):
        lp = tuple(p[l] for p in layer_params)
        xc, k_l, v_l, s_f, s_b = _trunk_layer(xc, c_ctx_b, lp, None, None)
        ks_l.append(k_l)
        vs_l.append(v_l)
        sf_l.append(s_f)
        sb_l.append(s_b)
    y_prompt = _rmsnorm(xc, final_norm_g)
    new_cache_k = jnp.stack(ks_l, axis=1)
    new_cache_v = jnp.stack(vs_l, axis=1)
    new_state_fwd = jnp.stack(sf_l, axis=1)
    new_state_bwd = jnp.stack(sb_l, axis=1)
    n_lat = x_sample.shape[1]
    rows = n_lat // GRID_W
    pos = (jnp.repeat(jnp.arange(rows), GRID_W), jnp.tile(jnp.arange(GRID_W), rows))
    xs = x_sample
    c_b = c[:, None, :]
    for l in range(DEPTH):
        lp = tuple(p[l] for p in layer_params)
        ctx = (cache_k[:, l], cache_v[:, l], state_fwd[:, l], state_bwd[:, l])
        xs, _, _, _, _ = _trunk_layer(xs, c_b, lp, ctx, pos)
    y_sample = _rmsnorm(xs, final_norm_g)
    return (y_prompt, y_sample, new_cache_k, new_cache_v, new_state_fwd, new_state_bwd)


_drawn_inputs = setup_inputs


def setup_inputs(seed=0):
    import zlib

    import numpy as np

    out = dict(_drawn_inputs(seed))
    spreads = {}
    factors = {'cache_k': 4.115,
     'cache_v': 3.453,
     'state_fwd': 8.0,
     'state_bwd': 8.0,
     'norm2_g': 8.0,
     'pool_scale': 3.285,
     'gla_gate_b_f': 8.0,
     'gla_gate_b_b': 8.0,
     'gla_norm_g': 8.0,
     'attn_sink': 8.0,
     'peer_wq': 8.0,
     'peer_subkeys': 8.0,
     'peer_u': 8.0,
     'peer_v': 8.0,
     'final_norm_g': 2.788}
    for name, (base, spread) in spreads.items():
        noise = np.random.default_rng([zlib.crc32(name.encode()), seed]).standard_normal(out[name].shape)
        drawn = base * np.exp(spread * noise) if base else spread * noise
        out[name] = jnp.asarray(drawn.astype(out[name].dtype))
    for name, factor in factors.items():
        out[name] = (out[name] * factor).astype(out[name].dtype)
    return out
```

```python
import numpy as np
import concourse.bass as bass
from concourse import mybir

F32 = mybir.dt.float32
BF16 = mybir.dt.bfloat16
U32 = mybir.dt.uint32
ALU = mybir.AluOpType
ACT = mybir.ActivationFunctionType
AX = mybir.AxisListType.X

P = 128
D = 1024
DEPTH = 2
KT = D // P
NB = 5
T = NB * P
TL = T - P
SEGS = ((0, P), (P, TL))
IN_W = 1824
HEADS, KVH, HD = 8, 2, 64
GH, GDK, GDV = 4, 32, 64
EPS = 1e-6
GRID_W = 64
NKEY = 128
TOPK = 16
PH = 8
SLOTS = PH * TOPK
N_EXP = NKEY * NKEY
RING = 8
ADA_RING = 4
ADA_CHUNK = 512
PAIRS = ((0, 1, 16), (1, 1, 8), (2, 1, 5), (3, 1, 4), (4, 1, 3), (5, 3, 2), (8, 8, 1))
NCAND = sum(n * m for _, n, m in PAIRS)
NEG = -3.0e38
C_POOL, C_GQ, C_GK, C_AQ, C_AK, C_GZ, C_GV, C_GG, C_AV = 0, 256, 384, 512, 1024, 1152, 1184, 1440, 1696
PAD = 8
PADW = T + 4 * PAD
PSEG = (PAD, 3 * PAD + P)


def build(nc, a, out, depth=DEPTH, stop_after=None):
    sems = []

    def sem(name):
        s = nc.alloc_semaphore(name)
        sems.append(s)
        return s

    def sb(name, width, dt=F32):
        return nc.alloc_sbuf_tensor(name, [P, width], dt)

    x = sb("x", NB * D)
    rows = sb("rows", NB * D)
    colsT = sb("colsT", KT * T)
    proj = sb("proj", 10176)
    modbc = sb("modbc", 8 * D)
    arena = sb("arena", 16 * D)
    modT = sb("modT", 96)
    cT = sb("cT", 16)
    cwork = sb("cwork", 32)
    ident = sb("ident", P)
    identb = sb("identb", P, BF16)
    ones = sb("ones", P)
    lofs = sb("lofs", 1)
    stats = sb("stats", 64)
    gmask = sb("gmask", 2 * P)
    amask = sb("amask", 2 * P, BF16)
    swapm = sb("swapm", P)
    edge = sb("edge", 34)
    small = sb("small", 128)
    iota50 = sb("iota50", NCAND)
    gates = sb("gates", NB * SLOTS)
    eidx = sb("eidx", NB * SLOTS, U32)
    ps = nc.alloc_psum_tensor("ps", [P, 8, 512], F32)
    modrow_d = nc.dram_tensor("modrow_d", (2, 6 * D), F32, kind="Internal").ap()

    xb = x[:, :].rearrange("p (b d) -> p b d", b=NB)
    rb = rows[:, :].rearrange("p (b d) -> p b d", b=NB)
    hT = colsT[:, :].rearrange("p (k t) -> p k t", k=KT)
    mT = modT[:, :].rearrange("p (v m k) -> p v m k", v=2, m=6)
    mb = modbc[:, :].rearrange("p (v m d) -> p v m d", v=2, m=4)
    G1, SH2, A2, G2 = range(4)

    def region(base, off, *dims):
        n = int(np.prod(dims))
        v = base[:, off:off + n]
        names = [f"d{i}" for i in range(len(dims))]
        if len(dims) > 1:
            v = v.rearrange("p (" + " ".join(names) + ") -> p " + " ".join(names), **dict(zip(names[1:], dims[1:])))
        return v

    def col(tile, off):
        return tile[:, off:off + 1]

    poolT = region(proj, 0, 2, PADW)
    gqT = region(proj, 1344, T)
    gkT = region(proj, 1984, T)
    gzT = region(proj, 2624, T)
    aqT = region(proj, 3264, 4, T)
    akT = region(proj, 5824, 7, P)
    gv = region(proj, 6720, NB, 256)
    gg = region(proj, 8000, NB, 256)
    av = region(proj, 9280, 7, P)
    qT = region(proj, 0, PH, T)
    w_in = region(arena, 0, KT, IN_W)
    rope = region(arena, KT * IN_W, 2, TL)
    w_out = region(arena, 0, KT, D)
    w_q = region(arena, KT * D, KT, D)
    mixT = hT
    pscale, gbias, sink8 = small[:, 0:2], small[:, 2:4], small[:, 4:12]

    def barrier():
        nc.all_engine_barrier(sems_to_clear=range(sems[0].num, sems[-1].num + 1))

    class Chain:

        def __init__(self, eng, s):
            self.eng, self.sem, self.n = eng, s, 0

        def done(self, ins):
            self.n += 1
            ins.then_inc(self.sem, 1)

        def wait(self):
            self.eng.wait_ge(self.sem, self.n)

        def link(self, ins):
            self.done(ins)
            self.wait()

    dve_step, act_step, pool_step = sem("dve_step"), sem("act_step"), sem("pool_step")
    loaded, stored = sem("loaded"), sem("stored")
    ev = {n: sem(n) for n in (
        "a_done b_done c_done d_done e_done f_done g_done h_done i_done j_done k_done l_done "
        "m_done n_done o_done p_done").split()}
    w_landed = [sem(f"w_landed{s}") for s in range(ADA_RING)]
    slot_u = [nc.alloc_semaphore(f"u_landed{r}") for r in range(RING)]
    slot_v = [nc.alloc_semaphore(f"v_landed{r}") for r in range(RING)]

    with nc.Block() as block:
        @block.sync
        def _(sp):
            loads = [(xb, a["x"].rearrange("b p d -> p b d")), (ident[:, :], a["ident"]), 
                     (gmask[:, :], a["gmask"]), (rows[:, 0:2 * P], a["amask"]), (swapm[:, :], a["swapm"]),
                     (edge[:, :], a["edge"]), (iota50[:, :], a["iota50"]), (cT[:, :], a["cT"])]
            for dst, src in loads:
                sp.dma_start(dst, src).then_inc(loaded, 16)
            sp.wait_ge(loaded, 16 * len(loads))

        @block.vector
        def _(dve):
            dve.memset(ones[:, :], 1.0).then_inc(ev["a_done"], 1)
            dve.memset(lofs[:, :], 0.0).then_inc(ev["a_done"], 1)
            dve.wait_ge(loaded, 16 * 8)
            dve.tensor_copy(identb[:, :], ident[:, :]).then_inc(ev["a_done"], 1)
            dve.tensor_copy(amask[:, :], rows[:, 0:2 * P]).then_inc(ev["a_done"], 1)
            dve.wait_ge(ev["a_done"], 4)
    barrier()

    def rstd_of(dve, act_sem, step, src, scale, n, off):
        m = stats[:, off:off + n]
        y = stats[:, off + n:off + 2 * n]
        z = stats[:, off + 2 * n:off + 3 * n]
        return m, y, z

    with nc.Fori(0, depth) as l:
        chunks = 6 * D // ADA_CHUNK
        ada = region(arena, 0, ADA_RING, KT, ADA_CHUNK)
        silu = cwork[:, 0:16].rearrange("p (k v) -> p k v", k=KT)
        mrow = modbc[0:2, 0:6 * D]
        brow = proj[0:2, 0:6 * D]
        nrow = proj[0:2, 6 * D:8 * D]
        chunk_mm, psum_free = ev["b_done"], ev["c_done"]
        silu_ready, mod_ready, cols_ready = ev["d_done"], ev["e_done"], ev["f_done"]
        with nc.Block() as block:
            @block.sync
            def _(sp):
                for dst, src in ((brow, a["b_ada"][l]), (nrow, a["nrow"][l]), (small[:, 0:4], a["small"][l]),
                                 (sink8, a["sink"][l])):
                    sp.dma_start(dst, src).then_inc(loaded, 16)
                wv = a["w_ada"].rearrange("l (k p) (c n) -> l c p k n", p=P, n=ADA_CHUNK)
                sp.sem_inc(chunk_mm, ADA_RING)
                with sp.Fori(0, chunks // ADA_RING) as i:
                    for s in range(ADA_RING):
                        sp.wait_ge(chunk_mm, i * ADA_RING + s + 1)
                        sp.dma_start(ada[:, s], wv[l, i * ADA_RING + s]).then_inc(w_landed[s], 16)
                sp.wait_ge(mod_ready, 1)
                sp.dma_start(modrow_d, mrow).then_inc(stored, 16)
                sp.wait_ge(stored, 16)
                sp.wait_ge(loaded, 64)

            @block.tensor
            def _(pe):
                pe.wait_ge(silu_ready, 1)
                with pe.Fori(0, chunks // ADA_RING) as i:
                    for s in range(ADA_RING):
                        pe.wait_ge(w_landed[s], i * 16 + 16)
                        pe.wait_ge(psum_free, i * ADA_RING + s + 1)
                        for k in range(KT):
                            mm = pe.matmul(ps[0:2, s, :], silu[:, k], ada[:, s, k], start=(k == 0), stop=(k == KT - 1))
                        mm.then_inc(chunk_mm, 1)
                pe.wait_ge(mod_ready, 1)
                for i in range(6 * KT):
                    mm = pe.transpose(ps[:, 7, 2 * i:2 * i + 2], mrow[:, i * P:(i + 1) * P], ident[0:2, 0:2])
                mm.then_inc(cols_ready, 1)

            @block.scalar
            def _(act):
                act.activation(cwork[:, 16:32], cT[:, :], ACT.Exp, scale=-1.0).then_inc(ev["h_done"], 1)

            @block.vector
            def _(dve):
                c = Chain(dve, dve_step)
                dve.sem_inc(psum_free, ADA_RING)
                dve.wait_ge(ev["h_done"], 1)
                c.link(dve.tensor_scalar(cwork[:, 16:32], cwork[:, 16:32], 1.0, None, ALU.add))
                c.link(dve.reciprocal(cwork[:, 16:32], cwork[:, 16:32]))
                dve.tensor_tensor(cwork[:, 0:16], cwork[:, 16:32], cT[:, :], ALU.mult).then_inc(silu_ready, 1)
                dve.wait_ge(loaded, 64)
                c.link(dve.tensor_scalar(sink8, sink8, HD ** 0.5, None, ALU.mult))
                with dve.Fori(0, chunks // ADA_RING) as i:
                    for s in range(ADA_RING):
                        dve.wait_ge(chunk_mm, ADA_RING + i * ADA_RING + s + 1)
                        cs = bass.ds((i * ADA_RING + s) * ADA_CHUNK, ADA_CHUNK)
                        dve.tensor_tensor(mrow[:, cs], ps[0:2, s, :], brow[:, cs], ALU.add).then_inc(psum_free, 1)
                dve.wait_ge(psum_free, ADA_RING + chunks)
                for m, n in ((1, 0), (4, 1)):
                    w = mrow[:, m * D:(m + 1) * D]
                    c.done(dve.scalar_tensor_tensor(out=w, in0=w, scalar=1.0, in1=nrow[:, n * D:(n + 1) * D], op0=ALU.add,
                                                    op1=ALU.mult))
                c.wait()
                dve.sem_inc(mod_ready, 1)
                dve.wait_ge(cols_ready, 1)
                c.link(dve.tensor_copy(modT[:, :].rearrange("p (v c) -> p v c", v=2),
                                       ps[:, 7, 0:96].rearrange("p (c v) -> p v c", v=2)))
        barrier()
        if stop_after == "ada":
            return

        ss, ms, yy, zz = stats[:, 0:5], stats[:, 5:10], stats[:, 10:15], stats[:, 15:20]

        def act_rstd(act, c, sum_ready, ms_ready, y_ready, ms, yy, zz):
            act.wait_ge(ms_ready, 1)
            c.link(act.activation(zz, ms, ACT.Ln))
            act.activation(yy, zz, ACT.Exp, scale=-0.5).then_inc(y_ready, 1)

        def dve_rstd(dve, c, sums, scale, ms_ready, y_ready, ms, yy, zz):
            c.link(dve.tensor_scalar(ms, sums, scale, EPS, ALU.mult, ALU.add))
            dve.sem_inc(ms_ready, 1)
            dve.wait_ge(y_ready, 1)
            c.link(dve.tensor_tensor(zz, yy, yy, ALU.mult))
            c.link(dve.tensor_tensor(zz, zz, ms, ALU.mult))
            c.link(dve.tensor_scalar(zz, zz, -0.5, 1.5, ALU.mult, ALU.add))
            c.link(dve.tensor_tensor(yy, yy, zz, ALU.mult))

        sums_ready, ms_ready, y_ready, xn_ready = ev["a_done"], ev["b_done"], ev["c_done"], ev["d_done"]
        tr_done, hT_act, hT_dve = ev["e_done"], ev["f_done"], ev["g_done"]
        mm_done, cp_act, cp_dve = ev["h_done"], ev["i_done"], ev["j_done"]
        pads_ready, swap_done, kc_done, kc_sb = ev["k_done"], ev["l_done"], ev["m_done"], ev["n_done"]

        col_tiles = [(c0, P) for c0 in range(0, C_GZ, P)] + [(C_GZ, 32)]

        def t_dst(i, seg):
            t0, n = SEGS[seg]
            c0, w = col_tiles[i]
            if c0 < C_GQ:
                return poolT[:, c0 // P, PSEG[seg]:PSEG[seg] + n]
            if c0 == C_GQ:
                return gqT[:, t0:t0 + n]
            if c0 == C_GK:
                return gkT[:, t0:t0 + n]
            if c0 < C_AK:
                return aqT[:, (c0 - C_AQ) // P, t0:t0 + n]
            if c0 == C_AK:
                return akT[:, 1 + t0 // P:1 + (t0 + n) // P].rearrange("p b t -> p (b t)")
            return gzT[0:32, t0:t0 + n]

        NT = len(col_tiles)
        with nc.Block() as block:
            @block.sync
            def _(sp):
                sp.dma_start(w_in, a["w_in"][l].rearrange("(k p) n -> p k n", p=P)).then_inc(loaded, 16)
                sp.dma_start(rope, a["rope"]).then_inc(loaded, 16)
                sp.wait_ge(kc_sb, 1)
                sp.dma_start(out["ck"][l], rows[:, 0:P]).then_inc(stored, 16)
                sp.dma_start(out["cv"][l], av[:, 1]).then_inc(stored, 16)
                sp.wait_ge(stored, 32)

            @block.gpsimd
            def _(pool):
                pool.memset(proj[:, 0:2 * PADW], 0.0).then_inc(pads_ready, 1)
                for z in (akT, av):
                    pool.memset(z[:, 0], 0.0).then_inc(pads_ready, 1)
                    pool.memset(z[:, 6], 0.0).then_inc(pads_ready, 1)

            @block.scalar
            def _(act):
                c = Chain(act, act_step)
                for b in range(NB):
                    act.activation(rb[:, b], xb[:, b], ACT.Square, accum_out=col(ss, b)).then_inc(sums_ready, 1)
                act_rstd(act, c, sums_ready, ms_ready, y_ready, ms, yy, zz)
                for k in range(KT):
                    act.wait_ge(tr_done, k + 1)
                    act.activation(hT[:, k, P:T], ps[:, 2 * (k % 4) + 1, :], ACT.Identity,
                                   scale=mT[:, 1, 1, k:k + 1], bias=mT[:, 1, 0, k:k + 1]).then_inc(hT_act, 1)
                act.wait_ge(pads_ready, 5)
                for i in range(NT):
                    act.wait_ge(mm_done, i + 1)
                    w = col_tiles[i][1]
                    d = t_dst(i, 1)
                    act.activation(d, ps[0:w, 2 * (i % 4) + 1, :], ACT.Copy,
                                   scale=GDK ** -0.5 if col_tiles[i][0] == C_GQ else 1.0).then_inc(cp_act, 1)
                for b in range(NB):
                    act.wait_ge(mm_done, NT + b + 1)
                    act.activation(av[:, 1 + b], ps[:, 2 * ((NT + b) % 4) + 1, 0:P], ACT.Copy).then_inc(cp_act, 1)

            @block.vector
            def _(dve):
                c = Chain(dve, dve_step)
                dve.wait_ge(sums_ready, NB)
                dve_rstd(dve, c, ss, 1.0 / D, ms_ready, y_ready, ms, yy, zz)
                for b in range(NB):
                    dve.tensor_scalar(rb[:, b], xb[:, b], col(yy, b), None, ALU.mult).then_inc(xn_ready, 1)
                for k in range(KT):
                    dve.wait_ge(tr_done, k + 1)
                    dve.tensor_scalar(hT[:, k, 0:P], ps[:, 2 * (k % 4), 0:P], mT[:, 0, 1, k:k + 1], mT[:, 0, 0, k:k + 1],
                                      ALU.mult, ALU.add).then_inc(hT_dve, 1)
                dve.wait_ge(pads_ready, 5)
                for i in range(NT):
                    dve.wait_ge(mm_done, i + 1)
                    w = col_tiles[i][1]
                    dve.tensor_scalar(t_dst(i, 0), ps[0:w, 2 * (i % 4), 0:P],
                                      GDK ** -0.5 if col_tiles[i][0] == C_GQ else 1.0, None,
                                      ALU.mult).then_inc(cp_dve, 1)
                for b in range(NB):
                    dve.wait_ge(mm_done, NT + b + 1)
                    bank = 2 * ((NT + b) % 4)
                    dve.tensor_copy(gv[:, b], ps[:, bank, 0:256]).then_inc(cp_dve, 1)
                    dve.tensor_copy(gg[:, b], ps[:, bank, 256:512]).then_inc(cp_dve, 1)
                dve.wait_ge(kc_done, 1)
                dve.tensor_copy(rows[:, 0:P], ps[:, 7, 256:256 + P]).then_inc(kc_sb, 1)
                for j in range(5):
                    v = aqT[:, j, P:T] if j < 4 else akT[:, 2:6].rearrange("p b t -> p (b t)")
                    dve.wait_ge(swap_done, j + 1)
                    w = rows[:, D:D + TL]
                    c.link(dve.tensor_tensor(w, ps[:, j, :], rope[:, 1], ALU.mult))
                    c.link(dve.tensor_tensor(v, v, rope[:, 0], ALU.mult))
                    c.link(dve.tensor_tensor(v, v, w, ALU.add))

            @block.tensor
            def _(pe):
                pe.wait_ge(xn_ready, NB)
                for k in range(KT):
                    if k >= 4:
                        pe.wait_ge(hT_act, k - 3)
                        pe.wait_ge(hT_dve, k - 3)
                    for b in range(NB):
                        dst = ps[:, 2 * (k % 4), 0:P] if b == 0 else ps[:, 2 * (k % 4) + 1, (b - 1) * P:b * P]
                        mm = pe.transpose(dst, rb[:, b, k * P:(k + 1) * P], ident[:, :])
                    mm.then_inc(tr_done, 1)
                pe.wait_ge(loaded, 32)
                pe.wait_ge(hT_act, KT)
                pe.wait_ge(hT_dve, KT)
                for i, (c0, w) in enumerate(col_tiles):
                    if i >= 4:
                        pe.wait_ge(cp_act, i - 3)
                        pe.wait_ge(cp_dve, i - 3)
                    for seg, (t0, n) in enumerate(SEGS):
                        for k in range(KT):
                            mm = pe.matmul(ps[0:w, 2 * (i % 4) + seg, 0:n], w_in[:, k, c0:c0 + w], hT[:, k, t0:t0 + n],
                                           start=(k == 0), stop=(k == KT - 1))
                    mm.then_inc(mm_done, 1)
                for b in range(NB):
                    i = NT + b
                    pe.wait_ge(cp_act, i - 3)
                    pe.wait_ge(cp_dve, i - 3 if b < 4 else NT + 2)
                    for c0, n, seg in ((C_GV, 512, 0), (C_AV, P, 1)):
                        for k in range(KT):
                            mm = pe.matmul(ps[:, 2 * (i % 4) + seg, 0:n], hT[:, k, b * P:(b + 1) * P],
                                           w_in[:, k, c0:c0 + n], start=(k == 0), stop=(k == KT - 1))
                    mm.then_inc(mm_done, 1)
                pe.wait_ge(cp_act, NT + NB)
                pe.wait_ge(cp_dve, NT + 2 * NB)
                pe.transpose(ps[:, 7, 256:256 + P], akT[:, 1], ident[:, :]).then_inc(kc_done, 1)
                for j in range(5):
                    v = aqT[:, j, P:T] if j < 4 else akT[:, 2:6].rearrange("p b t -> p (b t)")
                    pe.matmul(ps[:, j, :], swapm[:, :], v, start=True, stop=True).then_inc(swap_done, 1)
        barrier()
        if stop_after == "proj":
            return

        QF1, KF1, QB1, KB1, L2F, L3F, L2B, L3B, QF0, QB0, KFE, KBE = (region(arena, 8 * D + i * T, NB, P) for i in range(12))
        cF = region(modbc, 0, NB, P)
        eB = region(modbc, T, NB, P)
        tB = region(modbc, 2 * T, 8)
        laF, laB = region(modbc, 2 * T + 8, T), region(modbc, 3 * T + 8, T)
        l1w = region(modbc, 4 * T + 8, 2, T)
        oS = region(modbc, 6 * T + 8, NB, 256)
        oQ = region(modbc, 8 * T + 8, NB, 256)
        gnorm = region(modbc, 10 * T + 8, 256)
        bdm = region(modbc, 10 * T + 264, 256)
        totF = region(modbc, 10 * T + 520, 8)
        S = region(rows, 0, 10, 256)
        Pm = region(rows, 2560, 2, GH, P)
        Pw = region(rows, 3584, GH, P)
        kTok = region(rows, 4096, 2, P)
        pw = region(rows, 4352, 2, P)
        uw = region(rows, 4608, 256)
        gw2 = region(arena, 8 * D + 12 * T, 256)
        pools = region(arena, 8 * D, 2, PADW)
        log_mm, la_act, la_dve, mz_dve = ev["a_done"], ev["b_done"], ev["c_done"], ev["d_done"]
        d_ready, e_ready, qk_ready = ev["e_done"], ev["f_done"], ev["g_done"]
        pool_d, pool_mm = ev["h_done"], ev["i_done"]
        sc_done, P_ready, kt_done, kt_sb = ev["j_done"], ev["k_done"], ev["l_done"], ev["m_done"]
        u_done, S_ready, o_done = ev["n_done"], ev["o_done"], ev["p_done"]
        with nc.Block() as block:
            @block.sync
            def _(sp):
                for dst, src in ((gw2[0:32], a["gw2"][l]), (pw, a["pool_w"][l]), (S[:, 1], a["sf"][l]), (S[:, 8], a["sb"][l]),
                                 (bdm, a["bdm"]), (gnorm, a["gnorm"][l])):
                    sp.dma_start(dst, src).then_inc(loaded, 16)
                sp.dma_start(w_out, a["w_out"][l].rearrange("(k p) n -> p k n", p=P)).then_inc(loaded, 16)
                sp.wait_ge(loaded, 16 * 7)

            @block.gpsimd
            def _(pool):
                c = Chain(pool, pool_step)
                s = [region(arena, 8 * D, PADW), region(arena, 8 * D + PADW, PADW)]
                for t in range(2):
                    src = poolT[:, t]
                    c.link(pool.tensor_tensor(s[0][:, 1:PADW], src[:, 0:PADW - 1], src[:, 1:PADW], ALU.add))
                    hi = slice(64, 128)
                    if t == 0:
                        c.link(pool.tensor_tensor(s[1][64:128, 2:PADW - 1], s[0][64:128, 1:PADW - 2], s[0][64:128, 3:PADW], ALU.add))
                        parts = ((0, 64, s[0]), (64, 128, s[1]))
                    else:
                        c.link(pool.tensor_tensor(s[1][:, 2:PADW - 1], s[0][:, 1:PADW - 2], s[0][:, 3:PADW], ALU.add))
                        c.link(pool.tensor_tensor(s[0][:, 4:PADW - 3], s[1][:, 2:PADW - 5], s[1][:, 6:PADW - 1], ALU.add))
                        c.link(pool.tensor_tensor(s[1][64:128, 8:PADW - 7], s[0][64:128, 4:PADW - 11], s[0][64:128, 12:PADW - 3], ALU.add))
                        parts = ((0, 64, s[0]), (64, 128, s[1]))
                    for p0, p1, q in parts:
                        for seg, (t0, n) in enumerate(SEGS):
                            f = PSEG[seg]
                            c.done(pool.tensor_scalar(q[p0:p1, f:f + n], q[p0:p1, f:f + n], edge[p0:p1, 32 + t:33 + t], None, ALU.mult))
                    c.wait()
                    for p0, p1, q in parts:
                        for seg, (t0, n) in enumerate(SEGS):
                            f = PSEG[seg]
                            c.done(pool.tensor_tensor(q[p0:p1, f:f + 8], q[p0:p1, f:f + 8], edge[p0:p1, 16 * t:16 * t + 8], ALU.mult))
                            c.done(pool.tensor_tensor(q[p0:p1, f + n - 8:f + n], q[p0:p1, f + n - 8:f + n],
                                                      edge[p0:p1, 16 * t + 8:16 * t + 16], ALU.mult))
                    c.wait()
                    for p0, p1, q in parts:
                        for seg, (t0, n) in enumerate(SEGS):
                            f = PSEG[seg]
                            c.done(pool.tensor_tensor(src[p0:p1, f:f + n], q[p0:p1, f:f + n], src[p0:p1, f:f + n], ALU.subtract))
                    c.wait()
                pool.sem_inc(pool_d, 1)

            @block.tensor
            def _(pe):
                pe.wait_ge(loaded, 16 * 7)
                for dr in range(2):
                    for seg, (t0, n) in enumerate(SEGS):
                        mm = pe.matmul(ps[:, 2 * dr + seg, 0:n], gw2[0:32, dr * P:(dr + 1) * P], gzT[0:32, t0:t0 + n],
                                       start=True, stop=True)
                mm.then_inc(log_mm, 1)
                pe.wait_ge(pool_d, 1)
                for t in range(2):
                    for seg, (t0, n) in enumerate(SEGS):
                        mm = pe.matmul(ps[:, 4 + 2 * t + seg, 0:n], pw[:, t], poolT[:, t, PSEG[seg]:PSEG[seg] + n],
                                       start=True, stop=True)
                mm.then_inc(pool_mm, 1)
                pe.wait_ge(qk_ready, 1)
                pe.wait_ge(pool_mm, 2)
                ups = [(0, 0), (0, 1), (1, 0), (4, 1), (2, 0), (3, 1), (3, 0), (2, 1)]
                for i, (b, dr) in enumerate(ups):
                    if i >= 2:
                        pe.wait_ge(kt_sb, i - 1)
                    pe.transpose(ps[:, 4 + i % 2, 0:P], (KFE, KBE)[dr][:, b], ident[:, :]).then_inc(kt_done, 1)
                    pe.wait_ge(kt_sb, i + 1)
                    if i >= 2:
                        pe.wait_ge(S_ready, i - 1)
                    pe.matmul(ps[:, 6 + i % 2, 0:256], kTok[:, i % 2], gv[:, b], start=True, stop=True).then_inc(u_done, 1)
                pe.wait_ge(S_ready, len(ups))
                for b in range(NB):
                    if b >= 1:
                        pe.wait_ge(P_ready, b)
                    for h in range(GH):
                        r = slice(32 * h, 32 * h + 32)

                        def block_mm(k, q, s0, t0, n, c0=0):
                            return pe.matmul(ps[s0:s0 + n, h, c0 + t0:c0 + t0 + n], k[r, b, s0:s0 + n], q[r, b, t0:t0 + n],
                                             start=True, stop=True)
                        block_mm(L2F, L2F, 0, 64, 64)
                        block_mm(L2B, L2B, 64, 0, 64)
                        for g in (0, 64):
                            block_mm(L3F, L3F, g, g + 32, 32)
                            block_mm(L3B, L3B, g + 32, g, 32)
                        for g in range(0, P, 32):
                            block_mm(KF1, QF1, g, g, 32)
                        mm = pe.matmul(ps[:, h, P:2 * P], KB1[r, b], QB1[r, b], start=True, stop=True)
                    mm.then_inc(sc_done, 1)
                    pe.wait_ge(P_ready, b + 1)
                    for h in range(GH):
                        hs = slice(h * GDV, (h + 1) * GDV)
                        ob = ps[:, 4 + b % 4, hs]
                        if b >= 1:
                            pe.matmul(ob, QF0[:, b], S[:, b, hs], start=True, stop=False)
                            pe.matmul(ob, QB0[:, b], S[:, 4 + b, hs], start=False, stop=False)
                        mm = pe.matmul(ob, Pm[:, b % 2, h], gv[:, b, hs], start=(b == 0), stop=True)
                    mm.then_inc(o_done, 1)

            @block.scalar
            def _(act):
                c = Chain(act, act_step)
                act.wait_ge(la_dve, 4)
                c.done(act.activation(l1w[:, 0], laF, ACT.Abs))
                c.link(act.activation(l1w[:, 1], laB, ACT.Abs))
                c.link(act.activation(l1w, l1w, ACT.Exp, scale=-1.0))
                act.activation(l1w, l1w, ACT.Ln, bias=1.0).then_inc(la_act, 1)
                act.wait_ge(d_ready, 1)
                sc = 1.0 / 16.0
                lo, hi = slice(0, 64), slice(64, P)
                for dst, sgn in ((KF1, -1), (QF1, 1), (QB1, -1), (KB1, 1), (KFE, 1), (QB0, 1)):
                    act.activation(dst, dst, ACT.Exp, scale=sgn * sc).then_inc(e_ready, 1)
                act.activation(QF0, cF, ACT.Exp, scale=sc).then_inc(e_ready, 1)
                act.activation(KBE, eB, ACT.Exp, scale=sc).then_inc(e_ready, 1)
                act.activation(L2F[:, :, lo], L2F[:, :, lo], ACT.Exp, scale=-sc).then_inc(e_ready, 1)
                act.activation(L2F[:, :, hi], L2F[:, :, hi], ACT.Exp, scale=sc).then_inc(e_ready, 1)
                act.activation(L2B[:, :, lo], L2B[:, :, lo], ACT.Exp, scale=-sc).then_inc(e_ready, 1)
                act.activation(L2B[:, :, hi], L2B[:, :, hi], ACT.Exp, scale=sc).then_inc(e_ready, 1)
                for L in (L3F, L3B):
                    v = L.rearrange("p b (g w) -> p (b g) w", w=64)
                    act.activation(v[:, :, 0:32], v[:, :, 0:32], ACT.Exp, scale=-sc).then_inc(e_ready, 1)
                    act.activation(v[:, :, 32:64], v[:, :, 32:64], ACT.Exp, scale=sc).then_inc(e_ready, 1)
                act.activation(totF[:, 0:5], cF[:, :, 127], ACT.Exp, scale=sc).then_inc(e_ready, 1)
                act.activation(tB[:, 0:5], tB[:, 0:5], ACT.Exp, scale=sc).then_inc(e_ready, 1)

            @block.vector
            def _(dve):
                c = Chain(dve, dve_step)
                dve.wait_ge(log_mm, 1)
                for dr, la in ((0, laF), (1, laB)):
                    for seg, (t0, n) in enumerate(SEGS):
                        dve.tensor_scalar(la[:, t0:t0 + n], ps[:, 2 * dr + seg, 0:n], gbias[:, dr:dr + 1], None,
                                          ALU.add).then_inc(la_dve, 1)
                dve.wait_ge(la_act, 1)
                for dr, la in ((0, laF), (1, laB)):
                    c.done(dve.scalar_tensor_tensor(out=la, in0=la, scalar=0.0, in1=l1w[:, dr], op0=ALU.min, op1=ALU.subtract))
                c.wait()
                for b in range(NB):
                    for la, cc in ((laF, cF), (laB, eB)):
                        c.done(dve.tensor_tensor_scan(cc[:, b], ones[:, :], la[:, b * P:(b + 1) * P], 0.0, ALU.mult, ALU.add))
                c.wait()
                c.link(dve.tensor_copy(tB[:, 0:5], eB[:, :, 127]))
                c.link(dve.tensor_tensor(eB.rearrange("p b t -> p (b t)"), eB.rearrange("p b t -> p (b t)"), laB, ALU.subtract))
                dve.wait_ge(pool_d, 1)

                def refs(dst, cc, w, at):
                    n = T // w
                    v = lambda q: q.rearrange("p b (g w) -> p (b g) w", w=w)
                    return dve.tensor_tensor(v(dst), v(cc), v(cc)[:, :, at:at + 1].to_broadcast([P, n, w]), ALU.subtract)
                c.done(refs(QF1, cF, 32, 15))
                c.done(refs(KB1, eB, 32, 16))
                c.done(refs(L2F, cF, 128, 63))
                c.done(refs(L2B, eB, 128, 64))
                c.done(refs(L3F, cF, 64, 31))
                c.done(refs(L3B, eB, 64, 32))
                c.done(dve.tensor_tensor(KFE, cF[:, :, 127:128].to_broadcast([P, NB, P]), cF, ALU.subtract))
                c.done(dve.tensor_tensor(QB0, tB[:, 0:5].unsqueeze(2).to_broadcast([P, NB, P]), eB, ALU.subtract))
                c.wait()
                for s_, d_ in ((QF1, KF1), (KB1, QB1)):
                    c.link(dve.tensor_scalar(s_, s_, 1280.0, -1280.0, ALU.min, ALU.max))
                    c.link(dve.tensor_copy(d_, s_))
                dve.sem_inc(d_ready, 1)
                dve.wait_ge(e_ready, 18)
                q3 = gqT.rearrange("p (b t) -> p b t", b=NB)
                k3 = gkT.rearrange("p (b t) -> p b t", b=NB)
                for arr, w in ((QF1, q3), (KF1, k3), (QB1, q3), (KB1, k3), (QF0, q3), (QB0, q3), (KFE, k3), (KBE, k3)):
                    c.done(dve.tensor_tensor(arr, arr, w, ALU.mult))
                for arr, left, right in ((L2F, k3, q3), (L2B, q3, k3)):
                    c.done(dve.tensor_tensor(arr[:, :, 0:64], arr[:, :, 0:64], left[:, :, 0:64], ALU.mult))
                    c.done(dve.tensor_tensor(arr[:, :, 64:P], arr[:, :, 64:P], right[:, :, 64:P], ALU.mult))
                v = lambda q: q.rearrange("p b (g w) -> p (b g) w", w=64)
                for arr, left, right in ((L3F, k3, q3), (L3B, q3, k3)):
                    c.done(dve.tensor_tensor(v(arr)[:, :, 0:32], v(arr)[:, :, 0:32], v(left)[:, :, 0:32], ALU.mult))
                    c.done(dve.tensor_tensor(v(arr)[:, :, 32:64], v(arr)[:, :, 32:64], v(right)[:, :, 32:64], ALU.mult))
                c.wait()
                dve.sem_inc(qk_ready, 1)
                dve.wait_ge(pool_mm, 1)
                for t in range(2):
                    for seg, (t0, n) in enumerate(SEGS):
                        c.done(dve.tensor_scalar(mixT[:, t, t0:t0 + n], ps[:, 4 + 2 * t + seg, 0:n], pscale[:, t:t + 1], None, ALU.mult))
                c.wait()
                dve.sem_inc(pool_mm, 1)
                ups = [(0, 0), (0, 1), (1, 0), (4, 1), (2, 0), (3, 1), (3, 0), (2, 1)]
                dve.wait_ge(loaded, 16 * 7)
                for i, (b, dr) in enumerate(ups):
                    dve.wait_ge(kt_done, i + 1)
                    dve.tensor_copy(kTok[:, i % 2], ps[:, 4 + i % 2, 0:P]).then_inc(kt_sb, 1)
                    dve.wait_ge(u_done, i + 1)
                    c.wait()
                    if b == 0:
                        dve.tensor_tensor(S[:, 9 * dr], ps[:, 6 + i % 2, 0:256], bdm, ALU.mult).then_inc(S_ready, 1)
                        continue
                    c.link(dve.tensor_tensor(uw, ps[:, 6 + i % 2, 0:256], bdm, ALU.mult))
                    src, dst, dec = (b, b + 1, totF) if dr == 0 else (4 + b, 3 + b, tB)
                    dve.scalar_tensor_tensor(out=S[:, dst], in0=S[:, src], scalar=dec[:, b:b + 1], in1=uw,
                                             op0=ALU.mult, op1=ALU.add).then_inc(S_ready, 1)
                    dve.wait_ge(S_ready, i + 1)
                mF = gmask[:, 0:P].unsqueeze(1).to_broadcast([P, GH, P])
                mB = gmask[:, P:2 * P].unsqueeze(1).to_broadcast([P, GH, P])
                for b in range(NB):
                    dve.wait_ge(sc_done, b + 1)
                    if b >= 2:
                        dve.wait_ge(o_done, b - 1)
                    c.done(dve.tensor_tensor(Pm[:, b % 2], ps[:, 0:4, 0:P], mF, ALU.mult))
                    c.link(dve.tensor_tensor(Pw, ps[:, 0:4, P:2 * P], mB, ALU.mult))
                    dve.tensor_tensor(Pm[:, b % 2], Pm[:, b % 2], Pw, ALU.add).then_inc(P_ready, 1)
                    dve.wait_ge(P_ready, b + 1)
                    dve.wait_ge(o_done, b + 1)
                    c.link(dve.tensor_copy(oS[:, b], ps[:, 4 + b % 4, 0:256]))
        barrier()

        ssg, msg, yg, zg = (modbc[:, 7000 + i * 20:7020 + i * 20] for i in range(4))
        with nc.Block() as block:
            @block.sync
            def _(sp):
                for h in range(GH):
                    for o_, i_ in (("sf", 0), ("sb", 9)):
                        sp.dma_start(out[o_][l, h], S[32 * h:32 * h + 32, i_, h * GDV:(h + 1) * GDV]).then_inc(stored, 16)
                sp.wait_ge(stored, 16 * 2 * GH)

            @block.scalar
            def _(act):
                c = Chain(act, act_step)
                act.wait_ge(ev["a_done"], 1)
                act.activation(l1w[:, :, :].rearrange("p a t -> p (a t)"), gg.rearrange("p b c -> p (b c)"), ACT.Exp,
                               scale=-1.0).then_inc(ev["b_done"], 1)
                act_rstd(act, c, None, ev["c_done"], ev["d_done"], msg, yg, zg)

            @block.vector
            def _(dve):
                c = Chain(dve, dve_step)
                dve.sem_inc(ev["a_done"], 1)
                f = lambda q: q.rearrange("p b c -> p (b c)")
                h4 = lambda q: f(q).rearrange("p (g e) -> p g e", e=GDV)
                c.link(dve.tensor_tensor(f(oQ), f(oS), f(oS), ALU.mult))
                c.link(dve.tensor_reduce(ssg, h4(oQ), AX, ALU.add))
                dve_rstd(dve, c, ssg, 1.0 / GDV, ev["c_done"], ev["d_done"], msg, yg, zg)
                c.link(dve.tensor_tensor(h4(oS), h4(oS), yg.unsqueeze(2).to_broadcast([P, NB * GH, GDV]), ALU.mult))
                c.link(dve.tensor_tensor(oS, oS, gnorm.unsqueeze(1).to_broadcast([P, NB, 256]), ALU.mult))
                dve.wait_ge(ev["b_done"], 1)
                sg = l1w[:, :, :].rearrange("p a t -> p (a t)")
                c.link(dve.tensor_scalar(sg, sg, 1.0, None, ALU.add))
                c.link(dve.reciprocal(sg, sg))
                c.link(dve.tensor_tensor(sg, sg, f(gg), ALU.mult))
                c.link(dve.tensor_tensor(f(oS), f(oS), sg, ALU.mult))
                dve.sem_inc(ev["e_done"], 1)
                for t in range(2):
                    dve.wait_ge(ev["f_done"], t + 1)
                    c.done(dve.tensor_copy(mixT[:, 2 + t, 0:P], ps[:, 2 * t, 0:P]))
                    c.done(dve.tensor_copy(mixT[:, 2 + t, P:T], ps[:, 2 * t + 1, :]))
                c.wait()

            @block.tensor
            def _(pe):
                pe.wait_ge(ev["e_done"], 1)
                for t in range(2):
                    for b in range(NB):
                        dst = ps[:, 2 * t, 0:P] if b == 0 else ps[:, 2 * t + 1, (b - 1) * P:b * P]
                        mm = pe.transpose(dst, oS[:, b, t * P:(t + 1) * P], ident[:, :])
                    mm.then_inc(ev["f_done"], 1)
        barrier()
        if stop_after == "gla":
            return

        CACHE = -1
        keys = [[(1, None)]]
        for b in range(1, NB):
            row = []
            if b > 1:
                row.append((b, 0))
            row.append((b + 1, None))
            if b < NB - 1:
                row.append((b + 2, 1))
            keys.append(row + [(CACHE, None)])
        work = [(b, j + 4 * g) for b in range(NB) for j in range(4) for g in range(2)]
        NP_ = 3
        prob = region(modbc, 0, NP_, 4, P)
        probT = region(modbc, NP_ * 512, NP_, 4, P)
        yrow = region(modbc, 2 * NP_ * 512, 2, 512)
        ckT = region(rows, 0, P)
        cvr = region(rows, P, P)
        mx = region(rows, 256, 40)
        ngm = region(rows, 296, NB, 8)
        den = region(rows, 336, NB, 8)
        es = region(rows, 376, NB, 8)
        s_done, n_ready, p_ready, pt_done, pt_sb = (ev[k] for k in ("a_done", "b_done", "c_done", "d_done", "e_done"))
        o_done, y_ready, yt_done, yt_sb, es_ready = (ev[k] for k in ("f_done", "g_done", "h_done", "i_done", "j_done"))
        m_ready = ev["k_done"]
        with nc.Block() as block:
            @block.sync
            def _(sp):
                sp.dma_start(ckT, a["ckT"][l]).then_inc(loaded, 16)
                sp.dma_start(cvr, a["cv"][l]).then_inc(loaded, 16)
                sp.dma_start(w_q, a["w_q"][l].rearrange("(k p) n -> p k n", p=P)).then_inc(w_landed[0], 16)
                sp.wait_ge(w_landed[0], 16)

            @block.tensor
            def _(pe):
                pe.wait_ge(loaded, 32)

                def scores(i):
                    b, h = work[i]
                    r = slice(64 * (h // 4), 64 * (h // 4) + 64)
                    q = aqT[r, h % 4, b * P:(b + 1) * P]
                    if i >= 2:
                        pe.wait_ge(p_ready, i - 1)
                    for n, (kt, mk) in enumerate(keys[b]):
                        dst = ps[:, i % 2, n * P:(n + 1) * P]
                        k = ckT[r] if kt == CACHE else akT[r, kt]
                        mm = pe.matmul(dst, q, k, start=True, stop=mk is None)
                        if mk is not None:
                            mm = pe.matmul(dst, identb[:, :], amask[:, mk * P:(mk + 1) * P], start=False, stop=True)
                    mm.then_inc(s_done, 1)

                def turn(i):
                    b, h = work[i]
                    pe.wait_ge(p_ready, i + 1)
                    if i >= 2:
                        pe.wait_ge(pt_sb, i - 1)
                    for n in range(len(keys[b])):
                        mm = pe.transpose(ps[:, 2 + i % 2, n * P:(n + 1) * P], prob[:, i % NP_, n], ident[:, :])
                    mm.then_inc(pt_done, 1)

                def values(i):
                    b, h = work[i]
                    pe.wait_ge(pt_sb, i + 1)
                    if i % 8 == 0 and b >= 2:
                        pe.wait_ge(y_ready, b - 1)
                    g = h // 4
                    for n, (kt, mk) in enumerate(keys[b]):
                        vv = cvr if kt == CACHE else av[:, kt]
                        mm = pe.matmul(ps[:, 4 + b % 2, h * HD:(h + 1) * HD], probT[:, i % NP_, n],
                                       vv[:, g * HD:(g + 1) * HD], start=(n == 0), stop=(n == len(keys[b]) - 1))
                    mm.then_inc(o_done, 1)

                def turn_y(b):
                    pe.wait_ge(y_ready, b + 1)
                    if b >= 2:
                        pe.wait_ge(yt_sb, b - 1)
                    for t in range(4):
                        mm = pe.transpose(ps[:, 6 + b % 2, t * P:(t + 1) * P], yrow[:, b % 2, t * P:(t + 1) * P], ident[:, :])
                    mm.then_inc(yt_done, 1)

                n = len(work)
                for i in range(n + 2):
                    if i < n:
                        scores(i)
                    if 1 <= i <= n:
                        turn(i - 1)
                    if i >= 2:
                        values(i - 2)
                    if i >= 12 and (i - 12) % 8 == 0:
                        turn_y((i - 12) // 8)
                turn_y(NB - 1)

            @block.vector
            def _(dve):
                c = Chain(dve, dve_step)

                def head_max(i):
                    b, h = work[i]
                    dve.wait_ge(s_done, i + 1)
                    dve.tensor_reduce(mx[:, i:i + 1], ps[:, i % 2, 0:len(keys[b]) * P], AX, ALU.max).then_inc(m_ready, 1)
                    dve.wait_ge(m_ready, i + 1)
                    dve.tensor_scalar(ngm[:, b, h:h + 1], mx[:, i:i + 1], sink8[:, h:h + 1], -(HD ** -0.5), ALU.max,
                                      ALU.mult).then_inc(n_ready, 1)

                def copy_t(i):
                    b, h = work[i]
                    w = len(keys[b])
                    dve.wait_ge(pt_done, i + 1)
                    if i >= NP_:
                        dve.wait_ge(o_done, i - NP_ + 1)
                    dve.tensor_copy(probT[:, i % NP_, 0:w], ps[:, 2 + i % 2, 0:w * P].rearrange("p (n q) -> p n q", n=w)).then_inc(pt_sb, 1)

                def norm(b):
                    dve.wait_ge(es_ready, b + 1)
                    c.link(dve.tensor_tensor(den[:, b], den[:, b], es[:, b], ALU.add))
                    c.link(dve.reciprocal(den[:, b], den[:, b]))
                    dve.wait_ge(o_done, 8 * (b + 1))
                    if b >= 2:
                        dve.wait_ge(yt_done, b - 1)
                    dve.tensor_tensor(yrow[:, b % 2].rearrange("p (h e) -> p h e", h=HEADS),
                                      ps[:, 4 + b % 2, :].rearrange("p (h e) -> p h e", h=HEADS),
                                      den[:, b].unsqueeze(2).to_broadcast([P, HEADS, HD]), ALU.mult).then_inc(y_ready, 1)
                n = len(work)
                for i in range(n + 2):
                    if i < n:
                        head_max(i)
                    if 1 <= i <= n:
                        copy_t(i - 1)
                    if i >= 10 and (i - 10) % 8 == 0:
                        norm((i - 10) // 8)
                norm(NB - 1) if (n + 1 - 10) // 8 < NB - 1 else None

            @block.scalar
            def _(act):
                def exps(i):
                    b, h = work[i]
                    w = len(keys[b]) * P
                    act.wait_ge(n_ready, i + 1)
                    if i >= NP_:
                        act.wait_ge(pt_done, i - NP_ + 1)
                    act.activation(prob[:, i % NP_, 0:len(keys[b])].rearrange("p n q -> p (n q)"), ps[:, i % 2, 0:w], ACT.Exp,
                                   bias=ngm[:, b, h:h + 1], scale=HD ** -0.5, accum_out=den[:, b, h:h + 1]).then_inc(p_ready, 1)

                def copy_y(b):
                    act.wait_ge(yt_done, b + 1)
                    act.activation(mixT[:, 4:8, b * P:(b + 1) * P], ps[:, 6 + b % 2, :].rearrange("p (t q) -> p t q", t=4),
                                   ACT.Copy).then_inc(yt_sb, 1)
                c = Chain(act, act_step)
                for i in range(len(work)):
                    exps(i)
                    b = i // 8
                    if i % 8 == 7:
                        act.wait_ge(n_ready, i + 1)
                        act.wait_ge(p_ready, i + 1)
                        c.link(act.activation(es[:, b], sink8, ACT.Copy, scale=HD ** -0.5))
                        act.wait_ge(act_step, c.n)
                        for h in range(HEADS):
                            c.done(act.activation(es[:, b, h:h + 1], es[:, b, h:h + 1], ACT.Exp, bias=ngm[:, b, h:h + 1]))
                        c.wait()
                        act.sem_inc(es_ready, 1)
                    if i % 8 == 6 and b >= 1:
                        copy_y(b - 1)
                copy_y(NB - 1)
        barrier()
        if stop_after == "attn":
            return

        y_done, x_ready = ev["a_done"], ev["b_done"]
        sums_ready, ms_ready, yr_ready, h2_ready = ev["c_done"], ev["d_done"], ev["e_done"], ev["f_done"]
        tr_done, hT_act, hT_dve = ev["g_done"], ev["h_done"], ev["i_done"]
        q_done, q_act, q_dve = ev["j_done"], ev["k_done"], ev["l_done"]
        with nc.Block() as block:
            @block.sync
            def _(sp):
                src = bass.AP(tensor=modrow_d.tensor, offset=2 * D, ap=[[0, P], [6 * D, 2], [1, 4 * D]])
                sp.dma_start(modbc[:, :].rearrange("p (v n) -> p v n", v=2), src).then_inc(loaded, 16)
                sp.wait_ge(loaded, 16)

            @block.tensor
            def _(pe):
                for b in range(NB):
                    if b >= 4:
                        pe.wait_ge(x_ready, b - 3)
                    for n in range(2):
                        for k in range(KT):
                            mm = pe.matmul(ps[:, 2 * (b % 4) + n, :], mixT[:, k, b * P:(b + 1) * P],
                                           w_out[:, k, n * 512:(n + 1) * 512], start=(k == 0), stop=(k == KT - 1))
                    mm.then_inc(y_done, 1)
                pe.wait_ge(h2_ready, NB)
                for k in range(KT):
                    if k >= 4:
                        pe.wait_ge(hT_act, k - 3)
                        pe.wait_ge(hT_dve, k - 3)
                    for b in range(NB):
                        dst = ps[:, 2 * (k % 4), 0:P] if b == 0 else ps[:, 2 * (k % 4) + 1, (b - 1) * P:b * P]
                        mm = pe.transpose(dst, rb[:, b, k * P:(k + 1) * P], ident[:, :])
                    mm.then_inc(tr_done, 1)
                pe.wait_ge(hT_act, KT)
                pe.wait_ge(hT_dve, KT)
                for i in range(PH):
                    if i >= 4:
                        pe.wait_ge(q_act, i - 3)
                        pe.wait_ge(q_dve, i - 3)
                    for seg, (t0, n) in enumerate(SEGS):
                        for k in range(KT):
                            mm = pe.matmul(ps[:, 2 * (i % 4) + seg, 0:n], w_q[:, k, i * P:(i + 1) * P], hT[:, k, t0:t0 + n],
                                           start=(k == 0), stop=(k == KT - 1))
                    mm.then_inc(q_done, 1)

            @block.vector
            def _(dve):
                c = Chain(dve, dve_step)
                dve.wait_ge(loaded, 16)
                for b in range(NB):
                    v = min(b, 1)
                    dve.wait_ge(y_done, b + 1)
                    c.link(dve.tensor_tensor(rb[:, b], ps[:, 2 * (b % 4):2 * (b % 4) + 2, :].rearrange("p a n -> p (a n)"), mb[:, v, G1], ALU.mult))
                    dve.tensor_tensor(xb[:, b], xb[:, b], rb[:, b], ALU.add).then_inc(x_ready, 1)
                dve.wait_ge(sums_ready, NB)
                dve_rstd(dve, c, ss, 1.0 / D, ms_ready, yr_ready, ms, yy, zz)
                for b in range(NB):
                    v = min(b, 1)
                    c.link(dve.scalar_tensor_tensor(out=rb[:, b], in0=xb[:, b], scalar=col(yy, b), in1=mb[:, v, A2],
                                                    op0=ALU.mult, op1=ALU.mult))
                    dve.tensor_tensor(rb[:, b], rb[:, b], mb[:, v, SH2], ALU.add).then_inc(h2_ready, 1)
                for k in range(KT):
                    dve.wait_ge(tr_done, k + 1)
                    dve.tensor_copy(hT[:, k, 0:P], ps[:, 2 * (k % 4), 0:P]).then_inc(hT_dve, 1)
                for i in range(PH):
                    dve.wait_ge(q_done, i + 1)
                    dve.tensor_copy(qT[:, i, 0:P], ps[:, 2 * (i % 4), 0:P]).then_inc(q_dve, 1)

            @block.scalar
            def _(act):
                c = Chain(act, act_step)
                for b in range(NB):
                    act.wait_ge(x_ready, b + 1)
                    act.activation(rb[:, b], xb[:, b], ACT.Square, accum_out=col(ss, b)).then_inc(sums_ready, 1)
                act_rstd(act, c, sums_ready, ms_ready, yr_ready, ms, yy, zz)
                for k in range(KT):
                    act.wait_ge(tr_done, k + 1)
                    act.activation(hT[:, k, P:T], ps[:, 2 * (k % 4) + 1, :], ACT.Copy).then_inc(hT_act, 1)
                for i in range(PH):
                    act.wait_ge(q_done, i + 1)
                    act.activation(qT[:, i, P:T], ps[:, 2 * (i % 4) + 1, :], ACT.Copy).then_inc(q_act, 1)
        barrier()
        if stop_after == "q":
            return

        R2 = 2 * PH
        skT = region(arena, 0, PH, NKEY)
        sc = region(arena, 1024, R2, NKEY)
        sc2 = region(arena, 3072, R2, NKEY)
        sv = region(arena, 5120, R2, TOPK)
        siF = region(arena, 5376, R2, TOPK)
        cand = region(arena, 5632, PH, NCAND)
        cand2 = region(arena, 6032, PH, NCAND)
        cidx = region(arena, 6432, PH, NCAND)
        topv = region(arena, 6832, PH, TOPK)
        posF = region(arena, 6960, PH, TOPK)
        eF = region(arena, 7088, PH, TOPK)
        zs = region(arena, 7216, PH)
        rz = region(arena, 7224, PH)
        siU = region(arena, 7232, R2, TOPK).bitcast(U32)
        posU = region(arena, 7488, PH, TOPK).bitcast(U32)
        hot = region(arena, 8192, PH, TOPK, NCAND)
        s_done, sc_ready, sc_read, ex_in, ex_out = (ev[k] for k in ("a_done", "b_done", "c_done", "d_done", "e_done"))
        with nc.Block() as block:
            @block.sync
            def _(sp):
                sp.dma_start(skT, a["skT"][l]).then_inc(loaded, 16)
                sp.wait_ge(loaded, 16)

            @block.tensor
            def _(pe):
                pe.wait_ge(loaded, 16)
                for b in range(NB):
                    if b >= 2:
                        pe.wait_ge(sc_ready, b - 1)
                    for half in range(2):
                        r = slice(64 * half, 64 * half + 64)
                        for h in range(PH):
                            mm = pe.matmul(ps[:, 4 * (b % 2) + 2 * half + h // 4, (h % 4) * P:(h % 4 + 1) * P],
                                           qT[r, h, b * P:(b + 1) * P], skT[r, h], start=True, stop=True)
                    mm.then_inc(s_done, 1)

            @block.scalar
            def _(act):
                for b in range(NB):
                    act.wait_ge(s_done, b + 1)
                    if b >= 1:
                        act.wait_ge(sc_read, b)
                    act.activation(sc.rearrange("p r k -> p (r k)"),
                                   ps[:, 4 * (b % 2):4 * (b % 2) + 4, :].rearrange("p a n -> p (a n)"), ACT.Copy).then_inc(sc_ready, 1)
                    act.wait_ge(ex_in, b + 1)
                    act.activation(topv, topv, ACT.Exp).then_inc(ex_out, 1)

            @block.vector
            def _(dve):
                c = Chain(dve, dve_step)

                def top16(rows_, vals, spare, top, idx):
                    for r in range(rows_):
                        c.done(dve.max(top[:, r, 0:8], vals[:, r]))
                    c.wait()
                    for r in range(rows_):
                        c.done(dve.match_replace(spare[:, r], top[:, r, 0:8], vals[:, r], NEG))
                        c.done(dve.max_index(idx[:, r, 0:8], top[:, r, 0:8], vals[:, r]))
                    c.wait()
                    for r in range(rows_):
                        c.done(dve.max(top[:, r, 8:16], spare[:, r]))
                    c.wait()
                    for r in range(rows_):
                        c.done(dve.max_index(idx[:, r, 8:16], top[:, r, 8:16], spare[:, r]))
                    c.wait()

                for b in range(NB):
                    dve.wait_ge(sc_ready, b + 1)
                    top16(R2, sc, sc2, sv, siU)
                    dve.sem_inc(sc_read, 1)
                    c.link(dve.tensor_copy(siF, siU))
                    c.link(dve.tensor_scalar(siF[:, 0:PH], siF[:, 0:PH], float(NKEY), None, ALU.mult))
                    for lst, dst in ((sv, cand), (siF, cidx)):
                        at = 0
                        for i0, ni, nj in PAIRS:
                            c.done(dve.tensor_tensor(
                                dst[:, :, at:at + ni * nj].rearrange("p h (i j) -> p h i j", j=nj),
                                lst[:, 0:PH, i0:i0 + ni].unsqueeze(3).to_broadcast([P, PH, ni, nj]),
                                lst[:, PH:R2, 0:nj].unsqueeze(2).to_broadcast([P, PH, ni, nj]), ALU.add))
                            at += ni * nj
                    c.wait()
                    top16(PH, cand, cand2, topv, posU)
                    c.link(dve.tensor_copy(posF, posU))
                    c.link(dve.tensor_tensor(hot, iota50[:, :].unsqueeze(1).unsqueeze(1).to_broadcast([P, PH, TOPK, NCAND]),
                                             posF.unsqueeze(3).to_broadcast([P, PH, TOPK, NCAND]), ALU.is_equal))
                    c.link(dve.tensor_tensor(hot, hot, cidx.unsqueeze(2).to_broadcast([P, PH, TOPK, NCAND]), ALU.mult))
                    c.link(dve.tensor_reduce(eF, hot, AX, ALU.add))
                    c.link(dve.tensor_scalar(eidx[:, b * SLOTS:(b + 1) * SLOTS], eF.rearrange("p h k -> p (h k)"), lofs[:, 0:1], None, ALU.add))
                    c.link(dve.tensor_copy(zs, topv[:, :, 0]))
                    c.link(dve.tensor_tensor(topv, topv, zs.unsqueeze(2).to_broadcast([P, PH, TOPK]), ALU.subtract))
                    dve.sem_inc(ex_in, 1)
                    dve.wait_ge(ex_out, b + 1)
                    c.link(dve.tensor_reduce(zs, topv, AX, ALU.add))
                    c.link(dve.reciprocal(rz, zs))
                    c.link(dve.tensor_tensor(gates[:, b * SLOTS:(b + 1) * SLOTS].rearrange("p (h k) -> p h k", h=PH), topv,
                                             rz.unsqueeze(2).to_broadcast([P, PH, TOPK]), ALU.mult))
        barrier()
        if stop_after == "route":
            return

        uring = region(arena, 0, RING, D)
        vring = region(arena, RING * D, RING, D)
        junk = region(colsT, 0, D)
        y1 = region(colsT, D, D)
        dots = region(colsT, 2 * D, SLOTS)
        coef = region(colsT, 2 * D + SLOTS, SLOTS)
        dtmp = region(colsT, 2 * D + 2 * SLOTS, 16)
        diag = region(colsT, 2 * D + 3 * SLOTS, RING, P)
        zero = region(colsT, 2 * D + 3 * SLOTS + RING * P, P)
        hcur = region(colsT, 3584, D)
        stage_u = region(colsT, 3584 + D, 2 * RING).bitcast(U32)
        stage_v = region(colsT, 3584 + D + 2 * RING, 2 * RING).bitcast(U32)
        u_used, v_used, staged_u, staged_v = ev["a_done"], ev["b_done"], ev["c_done"], ev["n_done"]
        diag_ready, dots_ready, gelu_ready, coef_ready = ev["d_done"], ev["e_done"], ev["f_done"], ev["g_done"]
        y_open, y_done, y_read, dots_copied, zero_ready = (ev[k] for k in ("h_done", "i_done", "j_done", "k_done", "l_done"))
        hcur_ready = ev["m_done"]
        begun = ev["o_done"]
        tab_u, tab_v = a["peer_u"], a["peer_v"]
        GRP = 2 * RING
        NG = SLOTS // GRP

        def steps(eng, body):
            body(0, True, False)
            with eng.Fori(1, NB) as n:
                body(n, True, True)
            body(NB, False, True)

        with nc.Block() as block:
            @block.gpsimd
            def _(pool):
                def body(n, do_u, do_v):
                    with pool.Fori(0, NG) as g:
                        for half in range(2):
                            if do_u:
                                base = n * SLOTS + g * GRP + half * RING
                                pool.wait_ge(u_used, base + RING)
                                pool.tensor_copy(stage_u[:, half * RING:(half + 1) * RING], eidx[:, bass.ds(base, RING)]).then_inc(staged_u, 1)
                                pool.wait_ge(staged_u, (n * NG + g) * 2 + half + 1)
                            if do_v:
                                vbase = (n - 1) * SLOTS + g * GRP + half * RING
                                pool.wait_ge(v_used, vbase + RING)
                                pool.tensor_copy(stage_v[:, half * RING:(half + 1) * RING], eidx[:, bass.ds(vbase, RING)]).then_inc(staged_v, 1)
                                pool.wait_ge(staged_v, ((n - 1) * NG + g) * 2 + half + 1)
                            for r in range(RING):
                                if do_u:
                                    pool.wait_ge(u_used, base + r + 1)
                                    pool.sem_inc(begun, 1)
                                    pool.indirect_dma_start(uring[:, r], None, tab_u, bass.IndirectOffsetOnAxis(
                                        ap=stage_u[:, half * RING + r:half * RING + r + 1], axis=0)).then_inc(slot_u[r], 16)
                                if do_v:
                                    pool.wait_ge(v_used, vbase + r + 1)
                                    pool.sem_inc(begun, 1)
                                    pool.indirect_dma_start(vring[:, r], None, tab_v, bass.IndirectOffsetOnAxis(
                                        ap=stage_v[:, half * RING + r:half * RING + r + 1], axis=0)).then_inc(slot_v[r], 16)
                steps(pool, body)

            @block.vector
            def _(dve):
                dve.sem_inc(u_used, RING)
                dve.memset(zero, 0.0).then_inc(zero_ready, 1)

                def body(n, do_u, do_v):
                    if do_u:
                        dve.tensor_copy(hcur, rb[:, n]).then_inc(hcur_ready, 1)
                        dve.wait_ge(hcur_ready, n + 1)
                        dve.sem_inc(begun, 1)
                        with dve.Fori(0, NG) as g:
                            for half in range(2):
                                for r in range(RING):
                                    at = n * SLOTS + g * GRP + half * RING + r
                                    dve.wait_ge(slot_u[r], (((l * NB + n) * NG + g) * 2 + half) * 16 + 16)
                                    dve.tensor_tensor_reduce(
                                        out=junk, in0=uring[:, r], in1=hcur, scale=1.0, scalar=0.0, op0=ALU.mult,
                                        op1=ALU.add, accum_out=dtmp[:, half * RING + r:half * RING + r + 1]).then_inc(u_used, 1)
                                    dve.wait_ge(u_used, RING + at + 1)
                            dve.tensor_copy(dots[:, bass.ds(g * GRP, GRP)], dtmp).then_inc(dots_copied, 1)
                            dve.wait_ge(dots_copied, n * NG + g + 1)
                    if do_v:
                        dve.wait_ge(y_done, n)
                        yield_x(dve, n)
                    if do_u:
                        dve.sem_inc(dots_ready, 1)
                        dve.wait_ge(gelu_ready, n + 1)
                        dve.tensor_tensor(coef, dots, gates[:, bass.ds(n * SLOTS, SLOTS)], ALU.mult).then_inc(coef_ready, 1)
                        dve.wait_ge(coef_ready, n + 1)

                def yield_x(eng, n):
                    b = n - 1
                    gsrc = g2of(n)
                    yv = ps[:, 0:2, :].rearrange("p a n -> p (a n)")
                    eng.tensor_tensor(y1, yv, gsrc, ALU.mult).then_inc(y_read, 1)
                    eng.wait_ge(y_read, 2 * n - 1)
                    eng.tensor_tensor(xb[:, b], xb[:, b], y1, ALU.add).then_inc(y_read, 1)
                    eng.wait_ge(y_read, 2 * n)

                def g2of(n):
                    return mb[:, 0, G2] if g2of.first else mb[:, 1, G2]
                g2of.first = False
                body(0, True, False)
                g2of.first = True
                body(1, True, True)
                g2of.first = False
                with dve.Fori(2, NB) as n:
                    body(n, True, True)
                body(NB, False, True)
                dve.tensor_scalar(lofs[:, :], lofs[:, :], float(N_EXP), None, ALU.add).then_inc(dve_step, 1)
                dve.wait_ge(dve_step, 1)

            @block.scalar
            def _(act):
                def body(n, do_u, do_v):
                    if do_v:
                        with act.Fori(0, NG) as g:
                            for s in range(GRP):
                                at = (n - 1) * SLOTS + g * GRP + s
                                r = s % RING
                                act.wait_ge(v_used, at + 1)
                                act.activation(diag[:, r], ident[:, :], ACT.Copy,
                                               scale=coef[:, bass.ds(g * GRP + s, 1)]).then_inc(diag_ready, 1)
                    if do_u:
                        act.wait_ge(dots_ready, n + 1)
                        act.activation(dots, dots, ACT.Gelu).then_inc(gelu_ready, 1)
                        act.wait_ge(coef_ready, n + 1)
                steps(act, body)

            @block.tensor
            def _(pe):
                pe.sem_inc(v_used, RING)
                pe.wait_ge(zero_ready, 1)

                def body(n, do_u, do_v):
                    if not do_v:
                        return
                    pe.wait_ge(y_read, 2 * (n - 1)) if not (isinstance(n, int) and n == 1) else None
                    for c2 in range(2):
                        pe.matmul(ps[:, c2, :], zero, modbc[:, 0:512], start=True, stop=False)
                    with pe.Fori(0, NG) as g:
                        for s in range(GRP):
                            at = (n - 1) * SLOTS + g * GRP + s
                            r = s % RING
                            pe.wait_ge(slot_v[r], (((l * NB + n - 1) * NG + g) * 2 + s // RING) * 16 + 16)
                            pe.wait_ge(diag_ready, at + 1)
                            for c2 in range(2):
                                mm = pe.matmul(ps[:, c2, :], diag[:, r], vring[:, r, c2 * 512:(c2 + 1) * 512],
                                               start=False, stop=False)
                            mm.then_inc(v_used, 1)
                    for c2 in range(2):
                        mm = pe.matmul(ps[:, c2, :], zero, modbc[:, 0:512], start=False, stop=True)
                    mm.then_inc(y_done, 1)
                body(1, False, True)
                with pe.Fori(2, NB + 1) as n:
                    body(n, False, True)
        barrier()

    fg = region(proj, 0, D)
    sums_ready, ms_ready, y_ready, o_ready = ev["a_done"], ev["b_done"], ev["c_done"], ev["d_done"]
    with nc.Block() as block:
        @block.sync
        def _(sp):
            sp.dma_start(fg, a["fg"]).then_inc(loaded, 16)
            for b in range(NB):
                sp.wait_ge(o_ready, b + 1)
                sp.dma_start(out["y"][b], rb[:, b]).then_inc(stored, 16)
            sp.wait_ge(stored, 16 * NB)

        @block.scalar
        def _(act):
            c = Chain(act, act_step)
            for b in range(NB):
                act.activation(rb[:, b], xb[:, b], ACT.Square, accum_out=col(ss, b)).then_inc(sums_ready, 1)
            act_rstd(act, c, sums_ready, ms_ready, y_ready, ms, yy, zz)

        @block.vector
        def _(dve):
            c = Chain(dve, dve_step)
            dve.wait_ge(sums_ready, NB)
            dve_rstd(dve, c, ss, 1.0 / D, ms_ready, y_ready, ms, yy, zz)
            dve.wait_ge(loaded, 16)
            for b in range(NB):
                dve.scalar_tensor_tensor(out=rb[:, b], in0=xb[:, b], scalar=col(yy, b), in1=fg, op0=ALU.mult,
                                         op1=ALU.mult).then_inc(o_ready, 1)


def constants():
    ident = np.eye(P, dtype=np.float32)
    s, t = np.arange(P)[:, None], np.arange(P)[None, :]
    same = (s // 32) == (t // 32)
    gmask = np.concatenate([np.where(same, s <= t, True), same & (s >= t)], 1).astype(np.float32)
    amask = np.concatenate([np.where(t >= s, 0.0, -1e30), np.where(t <= s, 0.0, -1e30)], 1).astype(np.float32)
    swap = np.zeros((P, P), np.float32)
    swap[np.arange(P) ^ 16, np.arange(P)] = 1.0
    nf = HD // 4
    freqs = np.float32(10000.0) ** (-np.arange(nf, dtype=np.float32) / np.float32(nf))
    pos = np.arange(TL)
    p = np.arange(P)
    half, f = (p % 64) // 32, p % 16
    ang = np.where(half[:, None] == 0, (pos // GRID_W)[None], (pos % GRID_W)[None]).astype(np.float32) * freqs[f][:, None]
    sign = np.where((p % 32) < 16, -1.0, 1.0).astype(np.float32)[:, None]
    rope = np.stack([np.cos(ang), np.sin(ang) * sign], 1).astype(np.float32)
    edge = np.ones((P, 34), np.float32)
    for t_ in range(2):
        for q in range(P):
            win = 2 ** (1 + 2 * t_ + q // 64)
            left, right = win // 2, win - 1 - win // 2
            for e in range(8):
                edge[q, 16 * t_ + e] = win / (min(e, left) + 1 + right)
                after = 7 - e
                edge[q, 16 * t_ + 8 + e] = win / (left + 1 + min(after, right))
            edge[q, 32 + t_] = 1.0 / win
    bdm = np.kron(np.eye(GH), np.ones((GDK, GDV))).astype(np.float32)
    iota = np.tile(np.arange(NCAND, dtype=np.float32), (P, 1))
    return dict(ident=ident, gmask=gmask, amask=amask, swapm=swap, rope=rope, edge=edge,
                bdm=bdm, iota50=iota)


def layout(i):
    f = {k: np.ascontiguousarray(v) for k, v in i.items()}
    L = DEPTH

    def colsof(v, n):
        return v.reshape(L, n, P).transpose(0, 2, 1)

    cuts = np.cumsum([0, 256, 128, 128, 256, 256, 16, 16, 512, 128, 128])
    part = [np.arange(cuts[n], cuts[n + 1]) for n in range(10)]
    pool, gq, gk, gv, gg, gzf, gzb, aq, ak, av = part
    aq = aq.reshape(KVH, 4, HD).transpose(1, 0, 2).reshape(-1)
    order = np.concatenate([pool, gq, gk, aq, ak, gzf, gzb, gv, gg, av])
    d = {}
    d["x"] = np.concatenate([f["x_prompt"].reshape(1, P, D), f["x_sample"].reshape(4, P, D)], 0)
    d["cT"] = np.stack([f["c_ctx"].reshape(KT, P), f["c"].reshape(KT, P)], 2).transpose(1, 0, 2).reshape(P, 16)
    d["w_ada"] = f["w_ada"]
    d["b_ada"] = np.repeat(f["b_ada"][:, None], 2, 1)
    d["nrow"] = np.repeat(np.concatenate([f["norm1_g"], f["norm2_g"]], 1)[:, None], 2, 1)
    d["w_in"] = f["w_in"][:, :, order]
    pw = np.zeros((L, P, 2, P), np.float32)
    for g in range(4):
        o = 64 * (g % 2)
        pw[:, o:o + 64, g // 2, o:o + 64] = f["pool_w"][:, g]
    d["pool_w"] = pw
    d["small"] = np.concatenate([colsof(f["pool_scale"], 2), f["gla_gate_b_f"][:, :, None], f["gla_gate_b_b"][:, :, None]], 2)
    gw = np.zeros((L, 32, 256), np.float32)
    gw[:, 0:16, 0:128] = f["gla_gate_w_f"]
    gw[:, 16:32, 128:256] = f["gla_gate_w_b"]
    d["gw2"] = gw
    d["gnorm"] = np.repeat(f["gla_norm_g"][:, None, :], P, 1)
    d["sink"] = np.repeat(f["attn_sink"][:, None, :], P, 1)
    d["w_out"] = f["w_out"]
    d["w_q"] = f["peer_wq"]
    d["skT"] = f["peer_subkeys"].transpose(0, 2, 4, 1, 3).reshape(L, P, PH, NKEY)
    d["peer_u"] = f["peer_u"].reshape(L * N_EXP, D)
    d["peer_v"] = f["peer_v"].reshape(L * N_EXP, D)
    d["fg"] = np.repeat(f["final_norm_g"][None, :], P, 0)
    d["ckT"] = f["cache_k"][0].transpose(0, 2, 3, 1).reshape(L, P, P)
    d["cv"] = f["cache_v"][0].reshape(L, P, P)
    for n, s in (("sf", "state_fwd"), ("sb", "state_bwd")):
        z = np.zeros((L, P, 256), np.float32)
        for h in range(GH):
            z[:, 32 * h:32 * h + 32, 64 * h:64 * h + 64] = f[s][0, :, h]
        d[n] = z
    return {k: np.ascontiguousarray(v) for k, v in d.items()}


OUTS = {"y": (NB, P, D), "ck": (DEPTH, P, P), "cv": (DEPTH, P, P), "sf": (DEPTH, GH, GDK, GDV), "sb": (DEPTH, GH, GDK, GDV)}
DEBUG = {}


def kernel(**inputs):
    import concourse.bacc as _bacc
    from concourse.bass_utils import run_bass_kernel_spmd as _run

    arrays = {**layout(inputs), **constants()}
    nc = _bacc.Bacc("TRN2", target_bir_lowering=False, num_devices=1)
    a = {k: nc.dram_tensor("in_" + k, v.shape, mybir.dt.from_np(v.dtype), kind="ExternalInput").ap() for k, v in arrays.items()}
    o = {k: nc.dram_tensor("out_" + k, s, F32, kind="ExternalOutput").ap() for k, s in OUTS.items()}
    build(nc, a, o, **DEBUG)
    r = _run(nc, [{"in_" + k: v for k, v in arrays.items()}], core_ids=[0]).results[0]
    y = r["out_y"]
    return (y[0].reshape(1, P, D), y[1:].reshape(1, TL, D), r["out_ck"].reshape(1, DEPTH, P, KVH, HD),
            r["out_cv"].reshape(1, DEPTH, P, KVH, HD), r["out_sf"].reshape(1, DEPTH, GH, GDK, GDV),
            r["out_sb"].reshape(1, DEPTH, GH, GDK, GDV))
```
